# Optimizing a Trainium2 kernel written in Bass

```python
import math
import jax, jax.numpy as jnp
from jax import lax
import numpy as np

D_MODEL = 1024
BATCH = 1
SEQ = 128
DEPTH = 2
DEC_BATCH = 1
DEC_SEQ = 1024
PAST_LEN = 128

GRID_W = 64
EPS = 1e-6
H_A = 4
DK_A = 128
DV_A = 128
W_A = H_A * DV_A
CHUNK_A = 16
H_B = 4
DH_B = 64
DV_B = 2 * DH_B
W_B = H_B * DV_B
Q_BLOCK = 128
ROPE_BASE = 10000.0
G_C = 4
DG_C = 128
W_C = G_C * DG_C
N_BRANCH = 3
IN_SIZES = (H_A * DK_A, H_A * DK_A, H_A * DK_A, W_A, W_A,
            H_B * 2 * DH_B, H_B * 2 * DH_B, W_B, W_B,
            W_C, W_C, N_BRANCH * D_MODEL)
D_IN = 3 * H_A * DK_A + 2 * W_A + 4 * H_B * DH_B + 2 * W_B + 2 * W_C + N_BRANCH * D_MODEL

kernel_name = 'hybrid_hgrn2_diffattn_fnet_dit_step'

def rms_norm(x, g):
    xf = x.astype(jnp.float32)
    y = xf * lax.rsqrt(jnp.mean(xf * xf, axis=-1, keepdims=True) + EPS)
    return (y * g.astype(jnp.float32)).astype(x.dtype)

def rope_angles(pos):
    nf = DH_B // 4
    inv = ROPE_BASE ** (-jnp.arange(nf, dtype=jnp.float32) / nf)
    ang = pos[:, None] * inv[None, :]
    return jnp.cos(ang), jnp.sin(ang)

def axial_rope(x, rope):
    (cos_r, sin_r), (cos_c, sin_c) = rope
    half = DH_B // 2
    nf = half // 2
    xf = x.astype(jnp.float32)

    def rot(xa, cos, sin):
        cos = cos[None, :, None, None, :]
        sin = sin[None, :, None, None, :]
        x1, x2 = xa[..., :nf], xa[..., nf:]
        return jnp.concatenate([x1 * cos - x2 * sin, x1 * sin + x2 * cos], axis=-1)

    out = jnp.concatenate([rot(xf[..., :half], cos_r, sin_r),
                           rot(xf[..., half:], cos_c, sin_c)], axis=-1)
    return out.astype(x.dtype)

def hgrn2_chunked(q, k, logf, v, s0):
    B, T, H, _ = q.shape
    C = CHUNK_A
    N = T // C

    def chunks(a):
        return a.astype(jnp.float32).reshape(B, N, C, H, a.shape[-1])

    q, k, logf, v = chunks(q), chunks(k), chunks(logf), chunks(v)
    G = jnp.cumsum(logf, axis=2)
    lower = jnp.tril(jnp.ones((C, C), dtype=bool))[None, None, :, :, None, None]
    decay = jnp.exp(jnp.where(lower, G[:, :, :, None] - G[:, :, None, :], -jnp.inf))
    attn = jnp.einsum('bnthk,bnshk,bntshk->bnhts', q, k, decay)
    o_intra = jnp.einsum('bnhts,bnshv->bnthv', attn, v)
    g_end = G[:, :, -1]
    u = jnp.einsum('bnshk,bnshv->bnhkv', k * jnp.exp(g_end[:, :, None] - G), v)

    def step(s, inp):
        d_n, u_n = inp
        return d_n[..., None] * s + u_n, s

    s_fin, s_start = lax.scan(step, s0, (jnp.moveaxis(jnp.exp(g_end), 1, 0),
                                         jnp.moveaxis(u, 1, 0)))
    o_inter = jnp.einsum('bnthk,nbhkv->bnthv', q * jnp.exp(G), s_start)
    return (o_intra + o_inter).reshape(B, T, H, -1), s_fin

def diff_attention(q, k, v, lam):
    B, Tq = q.shape[0], q.shape[1]
    qb = jnp.moveaxis(q.reshape(B, Tq // Q_BLOCK, Q_BLOCK, H_B, 2, DH_B), 1, 0)

    def block(q_blk):
        s = jnp.einsum('bqhmd,bkhmd->bhmqk', q_blk, k).astype(jnp.float32)
        p = jax.nn.softmax(s, axis=-1)
        w = (p[:, :, 0] - lam * p[:, :, 1]).astype(v.dtype)
        return jnp.einsum('bhqk,bkhe->bqhe', w, v)

    o = lax.map(block, qb)
    return jnp.moveaxis(o, 0, 1).reshape(B, Tq, H_B, DV_B)

def fourier_mix(u):
    B, T, _ = u.shape
    ug = u.astype(jnp.float32).reshape(B, T, G_C, DG_C)
    f = jnp.fft.fft2(ug, axes=(1, 3), norm='ortho').real
    return f.reshape(B, T, W_C).astype(u.dtype)

def trunk_layer(x, cond, layer, lb, lw, ctx=None, rope=None):
    (ada_w, ada_b, norm_g, w_in, hgrn_g, qn_g, kn_g, lam_p, sub_g,
     w_br_a, w_br_b, w_br_c, w_out) = lw
    B, T, _ = x.shape
    mod = jax.nn.silu(cond) @ ada_w + ada_b
    shift, scale, gate = jnp.split(mod, 3, axis=-1)
    h = rms_norm(x, norm_g) * (1.0 + scale[:, None, :]) + shift[:, None, :]
    split_idx = np.cumsum(IN_SIZES)[:-1].tolist()
    qa, ffa, fba, ia, za, qb, kb, vb, zb, uc, zc, gts = jnp.split(h @ w_in, split_idx, axis=-1)

    q_a = jax.nn.silu(qa).reshape(B, T, H_A, DK_A)
    i_a = ia.reshape(B, T, H_A, DV_A)
    if ctx is None:
        s0 = jnp.zeros((B, 2, H_A, DK_A, DV_A), jnp.float32)
    else:
        s0 = ctx[2].astype(jnp.float32)
    o_dirs = []
    finals = []
    for d, fraw in enumerate((ffa, fba)):
        lbd = lb[d]
        logf = jnp.logaddexp(jnp.log(lbd), jnp.log1p(-lbd) + jax.nn.log_sigmoid(fraw.astype(jnp.float32)))
        logf = logf.reshape(B, T, H_A, DK_A)
        k_a = -jnp.expm1(logf)
        if d == 0:
            o_d, s_fin = hgrn2_chunked(q_a, k_a, logf, i_a, s0[:, 0])
        else:
            o_d, s_fin = hgrn2_chunked(q_a[:, ::-1], k_a[:, ::-1], logf[:, ::-1], i_a[:, ::-1], s0[:, 1])
            o_d = o_d[:, ::-1]
        o_dirs.append(o_d)
        finals.append(s_fin)
    o_a = rms_norm(o_dirs[0] + o_dirs[1], hgrn_g.reshape(H_A, DV_A)).astype(x.dtype)
    y_a = o_a.reshape(B, T, W_A) * jax.nn.silu(za)

    q_b = rms_norm(qb.reshape(B, T, H_B, 2, DH_B), qn_g)
    k_b = rms_norm(kb.reshape(B, T, H_B, 2, DH_B), kn_g)
    v_b = vb.reshape(B, T, H_B, DV_B)
    if ctx is None:
        k_all, v_all = k_b, v_b
    else:
        q_b = axial_rope(q_b, rope)
        k_all = jnp.concatenate([axial_rope(k_b, rope), ctx[0].astype(k_b.dtype)], axis=1)
        v_all = jnp.concatenate([v_b, ctx[1].astype(v_b.dtype)], axis=1)
    lam_init = 0.8 - 0.6 * math.exp(-0.3 * layer)
    lp = lam_p.astype(jnp.float32)
    lam = jnp.exp(jnp.sum(lp[0] * lp[1])) - jnp.exp(jnp.sum(lp[2] * lp[3])) + lam_init
    o_b = diff_attention(q_b * (DH_B ** -0.5), k_all, v_all, lam)
    y_b = (rms_norm(o_b, sub_g) * (1.0 - lam_init)).reshape(B, T, W_B) * jax.nn.silu(zb)

    y_c = fourier_mix(uc) * jax.nn.silu(zc)

    g = jax.nn.sigmoid(gts).reshape(B, T, N_BRANCH, D_MODEL)
    merged = (g[:, :, 0] * (y_a @ w_br_a) + g[:, :, 1] * (y_b @ w_br_b)
              + g[:, :, 2] * (y_c @ w_br_c))
    x_new = x + gate[:, None, :] * (merged @ w_out)
    if ctx is None:
        return x_new, k_b, v_b, jnp.stack(finals, axis=1)
    return x_new

def setup_inputs(seed: int = 0) -> dict:
    key = jax.random.key(seed)
    ks = jax.random.split(key, 21)
    f32 = jnp.float32
    n = lambda k, s: jax.random.normal(k, s, f32)
    return {
        'x_prompt': n(ks[0], (BATCH, SEQ, D_MODEL)),
        'x_sample': n(ks[1], (DEC_BATCH, DEC_SEQ, D_MODEL)),
        'c': n(ks[2], (DEC_BATCH, D_MODEL)),
        'cache_diff_k': n(ks[3], (DEC_BATCH, DEPTH, PAST_LEN, H_B, 2, DH_B)),
        'cache_diff_v': n(ks[4], (DEC_BATCH, DEPTH, PAST_LEN, H_B, DV_B)),
        'state_hgrn': 0.5 * n(ks[5], (DEC_BATCH, DEPTH, 2, H_A, DK_A, DV_A)),
        'c_ctx': n(ks[6], (D_MODEL,)),
        'ada_w': n(ks[7], (DEPTH, D_MODEL, 3 * D_MODEL)) * D_MODEL ** -0.5,
        'ada_b': 0.02 * n(ks[8], (DEPTH, 3 * D_MODEL)),
        'norm_g': 1.0 + 0.02 * n(ks[9], (DEPTH, D_MODEL)),
        'w_in': n(ks[10], (DEPTH, D_MODEL, D_IN)) * D_MODEL ** -0.5,
        'hgrn_lb': n(ks[11], (DEPTH, 2, H_A * DK_A)),
        'hgrn_norm_g': 1.0 + 0.02 * n(ks[12], (DEPTH, W_A)),
        'diff_qn_g': 1.0 + 0.02 * n(ks[13], (DEPTH, DH_B)),
        'diff_kn_g': 1.0 + 0.02 * n(ks[14], (DEPTH, DH_B)),
        'diff_lambda': 0.1 * n(ks[15], (DEPTH, 4, DH_B)),
        'diff_subln_g': 1.0 + 0.02 * n(ks[16], (DEPTH, DV_B)),
        'w_branch_a': n(ks[17], (DEPTH, W_A, D_MODEL)) * W_A ** -0.5,
        'w_branch_b': n(ks[18], (DEPTH, W_B, D_MODEL)) * W_B ** -0.5,
        'w_branch_c': n(ks[19], (DEPTH, W_C, D_MODEL)) * W_C ** -0.5,
        'w_out': n(ks[20], (DEPTH, D_MODEL, D_MODEL)) * D_MODEL ** -0.5,
    }

def reference(x_prompt, x_sample, c, cache_diff_k, cache_diff_v, state_hgrn, c_ctx,
              ada_w, ada_b, norm_g, w_in, hgrn_lb, hgrn_norm_g, diff_qn_g, diff_kn_g,
              diff_lambda, diff_subln_g, w_branch_a, w_branch_b, w_branch_c, w_out):
    lb_all = jnp.cumsum(jax.nn.softmax(hgrn_lb.astype(jnp.float32), axis=0), axis=0)
    lb_all = lb_all - lb_all[0]
    n_rows = x_sample.shape[1] // GRID_W
    pos_row = jnp.repeat(jnp.arange(n_rows, dtype=jnp.float32), GRID_W)
    pos_col = jnp.tile(jnp.arange(GRID_W, dtype=jnp.float32), n_rows)
    rope = (rope_angles(pos_row), rope_angles(pos_col))
    cond_ctx = jnp.broadcast_to(c_ctx, (x_prompt.shape[0], D_MODEL))

    xp = x_prompt
    xs = x_sample
    new_k, new_v, new_s = [], [], []
    for l in range(DEPTH):
        lw = (ada_w[l], ada_b[l], norm_g[l], w_in[l], hgrn_norm_g[l], diff_qn_g[l],
              diff_kn_g[l], diff_lambda[l], diff_subln_g[l], w_branch_a[l],
              w_branch_b[l], w_branch_c[l], w_out[l])
        xp, k_c, v_c, s_c = trunk_layer(xp, cond_ctx, l, lb_all[l], lw)
        new_k.append(k_c)
        new_v.append(v_c)
        new_s.append(s_c)
        xs = trunk_layer(xs, c, l, lb_all[l], lw,
                         ctx=(cache_diff_k[:, l], cache_diff_v[:, l], state_hgrn[:, l]),
                         rope=rope)
    new_cache_diff_k = jnp.stack(new_k, axis=1)
    new_cache_diff_v = jnp.stack(new_v, axis=1)
    new_state_hgrn = jnp.stack(new_s, axis=1)
    return (xp, xs, new_cache_diff_k, new_cache_diff_v, new_state_hgrn)


_drawn_inputs = setup_inputs


def setup_inputs(seed=0):
    import zlib

    import numpy as np

    out = dict(_drawn_inputs(seed))
    spreads = {}
    factors = {'cache_diff_k': 5.126,
     'cache_diff_v': 4.374,
     'state_hgrn': 32.2,
     'norm_g': 3.079,
     'hgrn_norm_g': 7.752,
     'diff_qn_g': 8.0,
     'diff_kn_g': 2.841,
     'diff_lambda': 8.0,
     'diff_subln_g': 8.0}
    for name, (base, spread) in spreads.items():
        noise = np.random.default_rng([zlib.crc32(name.encode()), seed]).standard_normal(out[name].shape)
        drawn = base * np.exp(spread * noise) if base else spread * noise
        out[name] = __import__('jax').numpy.asarray(drawn.astype(out[name].dtype))
    for name, factor in factors.items():
        out[name] = (out[name] * factor).astype(out[name].dtype)
    return out
```

```python
from contextlib import ExitStack
import math

import numpy as np

import concourse.bass as bass
from concourse import mybir

F32 = mybir.dt.float32
F32R = mybir.dt.float32r
U8 = mybir.dt.uint8
ALU = mybir.AluOpType
ACT = mybir.ActivationFunctionType
AX = mybir.AxisListType

P = 128
D_MODEL = 1024
DEPTH = 2
T_LAT = 1024
T_CTX = 128
T = T_LAT + T_CTX
GRID_W = 64
EPS = 1e-6
HEADS = 4
DH_B = 64
ROPE_BASE = 10000.0
KD = D_MODEL // P
TILE = 384
NT = T // TILE
CH = T // P
CL = T_LAT // P
CTX = CL
LEVELS = 7
KEYS = T

A0, B0, ZB0, MA0, MB0, C0, ZC0, MC0, O0, NBLK = 0, 20, 32, 36, 52, 68, 72, 76, 92, 100

IDENT, ONES, HEAD_ONES, ROT = range(4)
MASKS = 5

PC_LB = 0
PC_NG = PC_LB + DEPTH * 2 * HEADS
PC_HG = PC_NG + DEPTH * KD
PC_QN = PC_HG + DEPTH * HEADS
PC_KN = PC_QN + DEPTH
PC_SG = PC_KN + DEPTH
PC_AB = PC_SG + DEPTH
PC_LAM = PC_AB + DEPTH * 3 * KD
PC_C = PC_LAM + DEPTH * 4 * DH_B
PC_LI = PC_C + KD * 2
PC_ALL = PC_LI + DEPTH


def mixer_kernel(nc, x_in, w_full, w_half, ada_w, params, squares, masks, rope, dft_t, dft_c,
                 cache_k, cache_v, state_in, x_out, k_out, v_out, state_out):
    x_keep = nc.dram_tensor("x_keep", (KD, P, T), F32).ap()

    UNIT = 4 * T
    base = 16512
    off_h, off_x = base, base + 16 * UNIT
    off_y = off_x + 8 * UNIT
    off_w = off_y + 8 * UNIT
    off_c = off_w + 6 * 4096
    off_m = off_c + 4 * 512 + (MASKS + 1) * P
    off_p = off_m + 4 * 2 * DEPTH * 3 * KD

    def at(name, shape, dtype, offset):
        assert offset % 4 == 0
        return nc.alloc_sbuf_tensor_at(name, shape, dtype, offset=offset, align_bytes=4)

    h_hi = at("h_hi", [P, KD, T], F32R, off_h)
    h_lo = at("h_lo", [P, KD, T], F32R, off_h + 8 * UNIT)
    slabs = at("ada_slabs", [P, 6, 3 * D_MODEL], F32, off_h)
    X = at("X", [P, KD, T], F32, off_x)
    y_hi = at("y_hi", [P, HEADS, T], F32R, off_y)
    y_lo = at("y_lo", [P, HEADS, T], F32R, off_y + 4 * UNIT)
    w_raw = at("w_raw", [P, 2, KD * P], F32, off_w)
    w_hi = at("w_hi", [P, 2, KD, P], F32R, off_w + 8192)
    w_lo = at("w_lo", [P, 2, KD, P], F32R, off_w + 16384)
    sq_c = at("sq_c", [P, 4, P], F32, off_c)
    mask = at("mask", [P, MASKS + 1, P], U8, off_c + 4 * 512)
    mod = at("mod", [P, DEPTH, 3 * KD, 2], F32, off_m)
    par = at("par", [P, PC_ALL], F32, off_p)
    off_q = off_p + 4 * PC_ALL
    amul = at("amul", [P, DEPTH, KD, 2], F32, off_q)
    lbv = at("lbv", [P, DEPTH, 2, HEADS], F32, off_q + 128)
    oml = at("oml", [P, DEPTH, 2, HEADS], F32, off_q + 192)
    lam_n = at("lam_n", [P, DEPTH], F32, off_q + 256)
    gq = at("gq", [P, DEPTH], F32, off_q + 264)
    gsub = at("gsub", [P, DEPTH], F32, off_q + 272)
    lamw = at("lamw", [P, DEPTH, 2, DH_B], F32, off_y)
    lams = at("lams", [P, DEPTH, 2], F32, off_q + 280)
    epsc = at("epsc", [P, 1], F32, off_q + 296)
    lbt = at("lbt", [P, 4, 2, HEADS], F32, off_q + 304)
    stat = at("stat", [P, 3, 8], F32, off_q + 432)
    ptot = at("ptot", [P, 2, CH], F32, off_q + 528)
    off_s = off_q + 608
    assert off_s + 4 * UNIT + 2 * UNIT <= nc.sbuf_usable_end, (off_s, nc.sbuf_usable_end)
    SPACE = nc.sbuf_usable_end - off_s

    ident, ones, head_ones, rot_m = (sq_c[:, i, :] for i in range(4))

    a_q, a_ff, a_fb, a_at = (at(n, [P, T], F32, off_y + i * UNIT)
                             for n, i in (("a_q", 0), ("a_ff", 1), ("a_fb", 2), ("a_at", 7)))
    a_k2 = at("a_k2", [P, 2 * T], F32, off_y + 3 * UNIT)
    a_km = at("a_km", [P, 2, T], F32, off_s + 4 * UNIT + 1024)
    a_q2 = at("a_q2", [P, 2 * T], F32, off_y + 5 * UNIT)
    a_kf, a_kb = a_k2[:, 0:T], a_k2[:, T:2 * T]
    a_qb, a_qf = a_q2[:, 0:T], a_q2[:, T:2 * T]
    a_vt = at("a_vt", [P, T], F32, off_x + 4 * UNIT)
    a_v = at("a_v", [P, CH, P], F32, off_x + 5 * UNIT)
    a_ktf = at("a_ktf", [P, CH, P], F32, off_x + 6 * UNIT)
    a_ktb = at("a_ktb", [P, CH, P], F32, off_x + 7 * UNIT)
    a_sf = at("a_sf", [P, CL, P], F32, off_s)
    a_sb = at("a_sb", [P, CL, P], F32, off_s + 4096)
    a_sig = at("a_sig", [P, NT, TILE], F32, off_s + 8192)
    a_sq = at("a_sq", [P, T], F32, off_s + 6 * UNIT + 1024)
    a_rs = at("a_rs", [P, T], F32, off_s + 8192 + UNIT + 1024)
    a_kd = at("a_kd", [P, T], F32, off_s + 8192 + UNIT + 1024)
    a_fin = at("a_fin", [P, 2, P], F32, off_s + 8192 + UNIT)

    b_p = [at(f"b_p{i}", [P, 2, T], F32, o)
           for i, o in enumerate((off_y + 4 * UNIT, off_y + 6 * UNIT, off_s + 3 * UNIT + 1024))]
    b_wt = at("b_wt", [P, CH, 2 * P], F32, off_s)
    b_kh = at("b_kh", [P, 2, T + P], F32R, off_y)
    b_kl = at("b_kl", [P, T + P], F32R, off_y + 2 * UNIT + 1024)
    b_qs = at("b_qs", [P, 2, T], F32R, off_s + 5 * UNIT + 1024)
    b_raw = at("b_raw", [P, T], F32, off_y)
    b_sq = at("b_sq", [P, T], F32, off_y + UNIT)
    b_rs = at("b_rs", [P, T], F32, off_y + 2 * UNIT)
    b_raw2 = at("b_raw2", [P, T], F32, off_y + 3 * UNIT)
    b_n = at("b_n", [P, 2, T], F32, off_y + 4 * UNIT)
    b_vt = at("b_vt", [P, T], F32, off_y + 6 * UNIT)
    b_rc = at("b_rc", [P, T_LAT], F32, off_y + 7 * UNIT)
    b_q = at("b_q", [P, T], F32, off_s)
    b_k = at("b_k", [P, T + P], F32, off_s + UNIT)
    b_v = at("b_v", [P, CH + 1, P], F32, off_s + 2 * UNIT + 512)
    b_rope = at("b_rope", [P, 2, T_LAT], F32, off_s + 3 * UNIT + 1024)
    b_sq2 = at("b_sq2", [P, T], F32, off_s + 5 * UNIT + 1024)
    b_rs2 = at("b_rs2", [P, T], F32, off_s + 6 * UNIT + 1024)
    assert 7 * UNIT + 1024 <= SPACE

    c_u = at("c_u", [P, 2, T], F32, off_y)
    c_e = at("c_e", [P, 2, 4, P], F32, off_y + 2 * UNIT)
    c_z = at("c_z", [P, 8, P], F32, off_y + 2 * UNIT + 4096)
    c_s = at("c_s", [P, 4, P], F32, off_y + 2 * UNIT + 8192)
    c_ri = at("c_ri", [P, CH, 2 * P], F32, off_y + 2 * UNIT + 10240)
    c_t = at("c_t", [P, 3, 2 * P], F32, off_y + 4 * UNIT + 10240)
    c_c = at("c_c", [P, 2, CH, P], F32, off_s + 4 * UNIT)
    assert 4 * UNIT + 10240 + 3072 <= 8 * UNIT and 6 * UNIT <= SPACE
    yb = at("yb", [P, HEADS, T], F32, off_s)

    z_sq = at("z_sq", [P, 2, T], F32, off_y)
    z_rs = at("z_rs", [P, 2, T], F32, off_y + 2 * UNIT)
    z_sz = at("z_sz", [P, 2, T], F32, off_y + 4 * UNIT)
    m_g = at("m_g", [P, NT, TILE], F32, off_s + 4 * UNIT)
    m_p = at("m_p", [P, NT, TILE], F32, off_s + 5 * UNIT)
    n_sq = at("n_sq", [P, 2, T], F32, off_s + 4 * UNIT)
    n_rs = at("n_rs", [P, T], F32, off_s + 6 * UNIT)
    n_t = at("n_t", [P, 2, T], F32, off_y + 3 * UNIT)
    n_h = at("n_h", [P, 2, T], F32, off_y + 5 * UNIT)
    x_res = at("x_res", [P, KD, T], F32, off_y)
    cond = at("cond", [P, KD, 2], F32, off_s)
    mod_row = at("mod_row", [2, 3 * D_MODEL], F32, off_s + 1024)
    mask_in = at("mask_in", [P, MASKS + 1, P], F32, off_s + 1024 + 12 * D_MODEL)

    ctx = ExitStack()
    with ctx:
        ps = ctx.enter_context(nc.psum_tensor("ps", [P, 8, 512], F32))

        def sem(name):
            return ctx.enter_context(nc.semaphore(name))

        passed = sem("passed")
        const_in, rope_in, x_in_s = sem("const_in"), sem("rope_in"), sem("x_in")
        slab_in = [sem(f"slab_in{i}") for i in range(6)]
        w_loaded = [sem(f"w_loaded{s}") for s in range(2)]
        w_split = sem("w_split")
        w_hi_done = sem("w_hi_done")
        tile_done = [sem(f"tile_done{t}") for t in range(NT)]
        tile_free = [sem(f"tile_free{t}") for t in range(NT)]
        cond_ready, ada_mm, ada_row, ada_t, setup_done, eps_set = (
            sem(n) for n in ("cond_ready", "ada_mm", "ada_row", "ada_t", "setup_done", "eps_set"))
        lam_dot, lam_exp, lb_sub, lb_exp = (sem(n) for n in ("lam_dot", "lam_exp", "lb_sub", "lb_exp"))
        n_sq_s, n_sum, n_rs_s, n_xr, n_aff, n_hi, n_lo = (
            sem(n) for n in ("n_squares", "n_sums", "n_rstd", "n_scaled", "n_affine", "n_hi", "n_lo"))
        a_act, a_vt_s, a_kup, a_qup, a_mix, a_mm, a_vtok, a_kt_s, a_asm_act, a_asm, a_s_in, a_st, a_fin_s, a_fin_out = (
            sem(n) for n in ("a_gate", "a_vt", "a_k_level", "a_q_level", "a_k_mixed", "a_product", "a_vtok",
                             "a_kt", "a_rects", "a_assembled", "a_state_in", "a_states", "a_final",
                             "a_final_out"))
        a_free = [sem(f"a_bank_free{b}") for b in range(5)]
        b_raw_s, b_sum, b_rs_s, b_qn, b_rot, b_qk, b_vt_s, b_vtr, b_vtok, b_cache, b_kv_out, b_hi, b_lo = (
            sem(n) for n in ("b_squares", "b_sums", "b_rstd", "b_normed", "b_rotated", "b_qk",
                             "b_vt", "b_vtr", "b_vtok", "b_cache", "b_kv_out", "b_hi", "b_lo"))
        b_sc, b_max, b_exp, b_w, b_tr, b_ev = (
            sem(n) for n in ("b_scores", "b_max", "b_exp", "b_weights", "b_ring_done", "b_ring_free"))
        z_sq_s, z_sum, z_rs_s, z_act, z_done = (
            sem(n) for n in ("z_squares", "z_sums", "z_rstd", "z_silu", "z_done"))
        y_hi_s, y_lo_s = sem("y_hi_ready"), sem("y_lo_ready")
        m_gate, m_done = sem("m_gates"), sem("m_done")
        c_u_s, c_z_s, c_mm, c_ri_s, c_fin, c_out, c_tab = (
            sem(n) for n in ("c_u", "c_z", "c_products", "c_ri", "c_final", "c_out", "c_tables"))
        o_hi, o_lo, o_xin, o_res, o_store = (
            sem(n) for n in ("o_hi", "o_lo", "o_x_in", "o_residual", "o_store"))

        block = ctx.enter_context(nc.Block())
        SEGMENTS = ((0, T_LAT, 0), (T_LAT, T, 1))

        units = []
        units += [("diag", 0, g) for g in range(3)]
        for lev in range(LEVELS):
            units += [("level", lev, g) for g in range(3)]
            if lev == 0:
                units += [("vtok", 0, g) for g in range(3)]
        units += [(k, 0, g) for k in ("ktf", "ktb", "uf", "ub", "out", "sum") for g in range(3)]
        UNITS = len(units)
        unit_at = {u: i for i, u in enumerate(units)}
        uses = [sum(1 for i in range(UNITS) if i % 5 == b) for b in range(5)]

        def both_ways(pair, c, half):
            base = pair[:, c * P:c * P + 1]
            return bass.AP(base.tensor, base.offset, [base.ap[0], [2 * half, P // (2 * half)],
                                                      [T + half, 2], [1, half]])

        def alone(eng, semaphore, value, semaphore2=None, value2=None):
            eng.wait_ge(semaphore, value)
            if semaphore2 is not None:
                eng.wait_ge(semaphore2, value2)
            eng.sem_inc(passed, 1)

        @block.sync
        def _(sp):
            def fetch(n, slot, src, cols):
                sp.wait_ge(w_split, n)
                sp.dma_start(w_raw[:, slot, 0:cols], src).then_inc(w_loaded[slot], 16)

            with sp.Fori(0, DEPTH) as l:
                def fulls(first, count, at_n):
                    with sp.Fori(0, count // 2) as i:
                        for s in range(2):
                            fetch(l * NBLK + (i * 2 + (at_n + s)), s, w_full[l, i * 2 + (first + s)], KD * P)

                def merges(first, half, at_n):
                    with sp.Fori(0, KD) as j:
                        fetch(l * NBLK + (j * 2 + at_n), 0, w_full[l, j + first], KD * P)
                        fetch(l * NBLK + (j * 2 + at_n + 1), 1, w_half[l, j + half], 4 * P)

                fulls(0, 36, 0)
                merges(36, 0, MA0)
                merges(44, KD, MB0)
                fulls(52, 8, C0)
                merges(60, 2 * KD, MC0)
                fulls(68, 8, O0)

        @block.gpsimd
        def _(pool):
            pool.sem_inc(w_split, 1)

            def split(n, slot, kt):
                alone(pool, w_loaded[slot], n * 8 + (16 - 8 * slot), tile_done[NT - 1], n)
                raw = w_raw[:, slot, 0:kt * P].rearrange("p (k c) -> p k c", k=kt)
                pool.tensor_copy(w_hi[:, slot, 0:kt, :], raw).then_inc(w_hi_done, 1)
                pool.wait_ge(w_hi_done, n + 1)
                pool.tensor_tensor(w_lo[:, slot, 0:kt, :], raw, w_hi[:, slot, 0:kt, :].bitcast(F32),
                                   ALU.subtract).then_inc(w_split, 1)

            with pool.Fori(0, DEPTH) as l:
                def fulls(count, at_n):
                    with pool.Fori(0, count // 2) as i:
                        for s in range(2):
                            split(l * NBLK + (i * 2 + (at_n + s)), s, KD)

                def merges(at_n):
                    with pool.Fori(0, KD) as j:
                        split(l * NBLK + (j * 2 + at_n), 0, KD)
                        split(l * NBLK + (j * 2 + at_n + 1), 1, 4)

                fulls(36, 0)
                merges(MA0)
                merges(MB0)
                fulls(8, C0)
                merges(MC0)
                fulls(8, O0)

        @block.tensor
        def _(pe):
            for t in range(NT):
                pe.sem_inc(tile_done[t], 1)

            def product(slot, t, k, kt, hi, lo):
                cols = slice(t * TILE, (t + 1) * TILE)
                for i, (w, r) in enumerate(((w_hi, hi), (w_lo, hi), (w_hi, lo))):
                    mm = pe.matmul(ps[:, t, 0:TILE], w[:, slot, k, :], r[:, k, cols],
                                   start=(k == 0 and i == 0), stop=(k == kt - 1 and i == 2))
                return mm

            def project(n, slot, kt=KD, hi=h_hi, lo=h_lo, tiles=range(NT)):
                if tiles[0] == 0:
                    pe.wait_ge(w_split, n + 2)
                for t in tiles:
                    pe.wait_ge(tile_free[t], n)
                    for k in range(kt):
                        mm = product(slot, t, k, kt, hi, lo)
                    mm.then_inc(tile_done[t], 1)

            def project_as_split(n, slot, his, los):
                pe.wait_ge(w_split, n + 2)
                for t in range(NT):
                    pe.wait_ge(tile_free[t], n)
                for k in range(KD):
                    pe.wait_ge(his, l * KD + (k + 1))
                    pe.wait_ge(los, l * KD + (k + 1))
                    for t in range(NT):
                        mm = product(slot, t, k, KD, h_hi, h_lo)
                        if k == KD - 1:
                            mm.then_inc(tile_done[t], 1)

            def norm_sum(base, k):
                pe.wait_ge(n_sq_s, base + (k + 1))
                for t in range(NT):
                    mm = pe.matmul(ps[:, 3 + t, 0:TILE], ones, n_sq[:, k % 2, t * TILE:(t + 1) * TILE],
                                   start=(k == 0), stop=(k == KD - 1))
                mm.then_inc(n_sum, 1)

            pe.wait_ge(const_in, 48)
            for k in range(KD):
                norm_sum(0, k)
            pe.wait_ge(n_rs_s, NT)

            pe.wait_ge(cond_ready, 1)
            for l in range(DEPTH):
                if l:
                    pe.wait_ge(ada_row, l)
                for k in range(KD):
                    s = l * KD + k
                    pe.wait_ge(slab_in[s % 6], 16 * (s // 6 + 1))
                    for n in range(6):
                        mm = pe.matmul(ps[0:2, n, :], cond[:, k, :], slabs[:, s % 6, n * 512:(n + 1) * 512],
                                       start=(k == 0), stop=(k == KD - 1))
                    mm.then_inc(ada_mm, 1)
                pe.wait_ge(ada_row, l + 1)
                if l:
                    pe.wait_ge(setup_done, l)
                for j in range(3 * KD):
                    mm = pe.transpose(ps[:, 6, 2 * j:2 * j + 2], mod_row[0:2, j * P:(j + 1) * P],
                                      sq_c[0:2, IDENT, 0:2])
                mm.then_inc(ada_t, 1)

            with pe.Fori(0, DEPTH) as l:
                def head(h, hh):
                    n0 = l * NBLK + h * 5
                    a = l * HEADS + h
                    project_as_split(n0, hh, n_hi, n_lo)
                    for j in range(1, 4):
                        project(n0 + j, (hh + j) % 2)
                    for i, (kind, lev, g) in enumerate(units):
                        bank = 3 + i % 5
                        if kind == "diag" and g == 0:
                            pe.wait_ge(a_qup, a * 8 + 1)
                        if kind == "level" and g == 0:
                            pe.wait_ge(a_mix, a * LEVELS + lev + 1)
                            pe.wait_ge(a_qup, a * 8 + lev + 1)
                        if kind == "vtok" and g == 0:
                            pe.wait_ge(a_vt_s, a + 1)
                        if kind == "ktf" and g == 0:
                            pe.wait_ge(a_kup, a * 8 + 8)
                        if kind == "ktb" and g == 0:
                            pe.wait_ge(a_qup, a * 8 + 8)
                        if kind == "sum":
                            pe.wait_ge(z_sq_s, l * 24 + (h * 3 + (g + 1)))
                        if kind == "uf" and g == 0:
                            pe.wait_ge(a_vtok, a * 3 + 3)
                        if kind in ("uf", "ub"):
                            pe.wait_ge(a_kt_s, a * 6 + (kind == "ub") * 3 + g + 1)
                        if kind == "out" and g == 0:
                            pe.wait_ge(a_asm, a + 1)
                            pe.wait_ge(a_asm_act, a + 1)
                            pe.wait_ge(a_st, a + 1)
                        pe.wait_ge(a_free[i % 5], a * uses[i % 5] + i // 5)
                        for c in range(3 * g, 3 * g + 3):
                            o = ps[:, bank, (c % 3) * P:(c % 3 + 1) * P]
                            cs = slice(c * P, (c + 1) * P)
                            if kind == "diag":
                                mm = pe.matmul(o, a_kd[:, cs], a_q[:, cs], start=True, stop=True)
                            elif kind == "level":
                                mm = pe.matmul(o, a_km[:, lev % 2, cs], both_ways(a_q2, c, 1 << lev),
                                               start=True, stop=True)
                            elif kind == "vtok":
                                mm = pe.transpose(o, a_vt[:, cs], ident)
                            elif kind == "ktf":
                                mm = pe.transpose(o, a_kf[:, cs], ident)
                            elif kind == "ktb":
                                mm = pe.transpose(o, a_kb[:, cs], ident)
                            elif kind == "uf":
                                mm = pe.matmul(o, a_ktf[:, c, :], a_v[:, c, :], start=True, stop=True)
                            elif kind == "sum":
                                mm = pe.matmul(o, ones, a_sq[:, cs], start=True, stop=True)
                            elif kind == "ub":
                                mm = pe.matmul(o, a_ktb[:, c, :], a_v[:, c, :], start=True, stop=True)
                            else:
                                last = c == CTX
                                mm = pe.matmul(o, a_v[:, c, :], a_at[:, cs], start=True, stop=last)
                                if not last:
                                    pe.matmul(o, a_sf[:, c, :], a_qf[:, cs], start=False, stop=False)
                                    mm = pe.matmul(o, a_sb[:, c, :], a_qb[:, cs], start=False, stop=True)
                        mm.then_inc(a_mm, 1)
                        if kind == "level" and lev and g == 2:
                            t, first = (lev - 1) // 2, (lev - 1) % 2 * (KD // 2)
                            if lev == 1:
                                pe.wait_ge(w_split, n0 + 6)
                            if not first:
                                pe.wait_ge(tile_free[t], n0 + 4)
                            for k in range(first, first + KD // 2):
                                mm = product(hh, t, k, KD, h_hi, h_lo)
                            if first:
                                mm.then_inc(tile_done[t], 1)

                with pe.Fori(0, HEADS // 2) as hp:
                    for hh in range(2):
                        head(hp * 2 + hh, hh)

                def tails(n_first, count0, normed):
                    for s in range(HEADS):
                        if normed:
                            for t in range(NT):
                                pe.wait_ge(z_sq_s, l * 24 + (count0 + 3 * s + t + 1))
                                if s:
                                    pe.wait_ge(z_rs_s, l * 24 + (count0 + 3 * s))
                                pe.matmul(ps[:, 3 + t, 0:TILE], ones, z_sq[:, s % 2, t * TILE:(t + 1) * TILE],
                                          start=True, stop=True).then_inc(z_sum, 1)
                        project(l * NBLK + (n_first + s), s % 2)

                with pe.Fori(0, HEADS // 2) as hp:
                    for hh in range(2):
                        a = l * HEADS + (hp * 2 + hh)
                        n0 = l * NBLK + (hp * 6 + (B0 + 3 * hh))
                        project(n0, hh % 2)
                        project(n0 + 1, (hh + 1) % 2)
                        for m, (sq, banks) in enumerate(((b_sq, (3, 4, 5)), (b_sq2, (6, 7, 3)))):
                            for t in range(NT):
                                pe.wait_ge(b_raw_s, a * 6 + (3 * m + t + 1))
                                if m and banks[t] == 3:
                                    pe.wait_ge(b_rs_s, a * 6 + 1)
                                pe.matmul(ps[:, banks[t], 0:TILE], head_ones, sq[:, t * TILE:(t + 1) * TILE],
                                          start=True, stop=True).then_inc(b_sum, 1)
                        project(n0 + 2, hh % 2, tiles=(0,))
                        for m in range(2):
                            pe.wait_ge(b_rs_s, a * 6 + (3 if m == 0 else 5))
                            pe.wait_ge(b_qn, a * 2 + (m + 1))
                            for i in range(2):
                                pe.matmul(ps[:, 4 + 2 * m + i, :], rot_m, b_n[:, m, i * 512:(i + 1) * 512],
                                          start=True, stop=True).then_inc(b_rot, 1)
                        project(n0 + 2, hh % 2, tiles=(1, 2))
                        pe.wait_ge(b_vt_s, a + 1)
                        for g in range(3):
                            for c in range(3 * g, 3 * g + 3):
                                mm = pe.transpose(ps[:, g, (c % 3) * P:(c % 3 + 1) * P],
                                                  b_vt[:, c * P:(c + 1) * P], ident)
                            mm.then_inc(b_vtr, 1)
                        pe.wait_ge(b_lo, a + 1)
                        pe.wait_ge(b_hi, a * 3 + 3)
                        pe.wait_ge(b_cache, 32 * a + 32)
                        pe.wait_ge(b_vtok, a * 3 + 3)

                        ring = 0

                        def ring_bank():
                            nonlocal ring
                            ring += 1
                            return ps[:, 6 + (ring - 1) % 2]

                        def transposed(i, g):
                            if g == 0:
                                pe.wait_ge(b_w, a * CH + (i + 1))
                            if ring > 1:
                                pe.wait_ge(b_ev, a * 30 + (ring - 1))
                            o = ring_bank()
                            for c in range(1 if i == CTX else 3):
                                kt = 3 * g + c
                                mm = pe.transpose(o[:, c * P:(c + 1) * P],
                                                  b_p[i % 3][:, 0, kt * P:(kt + 1) * P], ident)
                            mm.then_inc(b_tr, 1)

                        def values(i):
                            pe.wait_ge(b_ev, a * 30 + ring)
                            o = ring_bank()
                            wide = P if i == CTX else 2 * P
                            for kt in range(1 if i == CTX else CH):
                                vt = CH if i == CTX else kt
                                mm = pe.matmul(o[:, 0:wide], b_v[:, vt, :], b_wt[:, kt, 0:wide],
                                               start=(kt == 0), stop=(kt == CH - 1 or i == CTX))
                            mm.then_inc(b_tr, 1)

                        def scores(i, m):
                            if i:
                                pe.wait_ge(b_exp, a * 18 + (2 * i + m - 1))
                            rows = slice(m * DH_B, (m + 1) * DH_B)
                            qs = slice(i * P, (i + 1) * P)
                            for t in range(1 if i == CTX else NT):
                                ks = slice(T, T + P) if i == CTX else slice(t * TILE, (t + 1) * TILE)
                                o = ps[:, 3 * m + t, 0:ks.stop - ks.start]
                                pe.matmul(o, b_qs[:, m, qs], b_kh[:, m, ks], start=True, stop=False)
                                mm = pe.matmul(o, b_qs[rows, m, qs], b_kl[rows, ks], start=False, stop=True)
                            mm.then_inc(b_sc, 1)

                        for i in range(CH):
                            scores(i, 0)
                            if i % 2 == 0 and i >= 4:
                                values(i - 3)
                            if i >= 2:
                                transposed(i - 2, 0)
                                transposed(i - 2, 1)
                            scores(i, 1)
                            if i >= 2:
                                transposed(i - 2, 2)
                        for g in range(3):
                            transposed(CTX - 1, g)
                        values(CTX - 1)
                        transposed(CTX, 0)
                        values(CTX)
                        assert ring == 30
                tails(ZB0, 12, True)

                def merge(n_first, order):
                    with pe.Fori(0, KD) as j:
                        n = l * NBLK + (j * 2 + n_first)
                        project(n, 0)
                        pe.wait_ge(y_lo_s, l * 12 + 4 * (order + 1))
                        pe.wait_ge(y_hi_s, l * 12 + 4 * (order + 1))
                        project(n + 1, 1, 4, y_hi, y_lo)

                merge(MA0, 0)
                merge(MB0, 1)

                with pe.Fori(0, HEADS // 2) as gp:
                    for s in range(2):
                        project(l * NBLK + (gp * 2 + (C0 + s)), s)
                    for s in range(2):
                        g1 = l * HEADS + (gp * 2 + s)
                        if s == 0:
                            pe.wait_ge(c_tab, l * 32 + 32)
                        pe.wait_ge(c_z_s, g1 + 1)
                        parts = ((0, None, 0), (2, 4, 2), (6, 7, 2), (3, 5, 1),
                                 (1, None, 0), (3, 5, 2), (6, 7, 1), (2, 4, 1))
                        for d2 in range(4):
                            pe.wait_ge(c_out, g1 * 3)
                            for dd in range(2):
                                re, im, tab = parts[2 * d2 + dd]
                                o = ps[:, 3 + d2, dd * 256:(dd + 1) * 256]
                                mm = pe.matmul(o, c_z[:, re, :], c_t[:, 0, :], start=True, stop=im is None)
                                if im is not None:
                                    mm = pe.matmul(o, c_z[:, im, :], c_t[:, tab, :], start=False, stop=True)
                            mm.then_inc(c_mm, 1)
                        mm = pe.matmul(ps[:, 7, 0:256], c_u[:, s, T_LAT:T], c_t[:, 0, :], start=True, stop=True)
                        mm.then_inc(c_mm, 1)
                        pe.wait_ge(c_ri_s, g1 * 5 + 5)
                        for d in range(CH):
                            o = ps[:, 3 + d // 4, (d % 4) * P:(d % 4 + 1) * P]
                            pe.matmul(o, c_ri[:, d, 0:P], c_c[:, 0, d, :], start=True, stop=False)
                            mm = pe.matmul(o, c_ri[:, d, P:2 * P], c_c[:, 1, d, :], start=False, stop=True)
                            if d in (3, 7, 8):
                                mm.then_inc(c_fin, 1)
                tails(ZC0, 0, False)
                merge(MC0, 2)

                for j in range(KD // 2):
                    if j == 0:
                        project_as_split(l * NBLK + O0, 0, o_hi, o_lo)
                    else:
                        project(l * NBLK + (j * 2 + O0), 0)
                    project(l * NBLK + (j * 2 + (O0 + 1)), 1)
                    if j:
                        for k in (2 * j - 2, 2 * j - 1):
                            norm_sum(l * KD + KD, k)
                for k in (KD - 2, KD - 1):
                    norm_sum(l * KD + KD, k)

        @block.scalar
        def _(act):
            act.dma_start(par[:, :], params).then_inc(const_in, 16)
            act.dma_start(sq_c[:, :, :], squares).then_inc(const_in, 16)
            act.dma_start(mask_in[:, :, :], masks).then_inc(const_in, 16)
            act.dma_start(X[:, :, :], x_in).then_inc(x_in_s, 16)

            def rstd(out, bank, scale, done):
                act.activation(out, ps[:, bank, 0:TILE], ACT.Ln, bias=epsc[:, 0:1], scale=scale)
                act.drain()
                act.activation(out, out, ACT.Exp, scale=-0.5).then_inc(done, 1)

            def norm_square(base, k, tile):
                if k >= 2:
                    act.wait_ge(n_sum, base + (k - 1))
                act.activation(n_sq[:, k % 2, :], tile, ACT.Square).then_inc(n_sq_s, 1)

            def norm_rstd(base):
                act.preload_act_table_set("natural_log_exp_and_others")
                for t in range(NT):
                    if t == 0:
                        act.wait_ge(n_sum, base + KD)
                    rstd(n_rs[:, t * TILE:(t + 1) * TILE], 3 + t, 1.0 / D_MODEL, n_rs_s)

            for s in range(DEPTH * KD):
                if s == 6:
                    act.wait_ge(eps_set, 1)
                    act.wait_ge(x_in_s, 16)
                    for k in range(KD):
                        norm_square(0, k, X[:, k, :])
                    norm_rstd(0)
                    act.wait_ge(const_in, 48)
                    act.activation(cond[:, :, :].rearrange("p k c -> p (k c)"), par[:, PC_C:PC_C + 2 * KD],
                                   ACT.Silu).then_inc(cond_ready, 1)
                if s >= 6:
                    act.wait_ge(ada_mm, s - 5)
                if s == KD + 5:
                    act.activation(mod_row[:, :].rearrange("p (a b) -> p a b", a=6), ps[0:2, 0:6, :],
                                   ACT.Copy).then_inc(ada_row, 1)
                act.dma_start(slabs[:, s % 6, :], ada_w[s // KD, (s % KD) * P:(s % KD + 1) * P, :]).then_inc(slab_in[s % 6], 16)
            act.wait_ge(ada_mm, DEPTH * KD)
            act.wait_ge(ada_t, 1)
            act.activation(mod_row[:, :].rearrange("p (a b) -> p a b", a=6), ps[0:2, 0:6, :],
                           ACT.Copy).then_inc(ada_row, 1)
            act.wait_ge(lb_sub, 1)
            act.activation(lbt[:, 0:2, :, :], lbt[:, 0:2, :, :], ACT.Exp).then_inc(lb_exp, 1)
            act.wait_ge(lam_dot, 1)
            act.activation(lams[:, :, :], lams[:, :, :], ACT.Exp).then_inc(lam_exp, 1)
            act.dma_start(x_keep.rearrange("k p t -> p k t"), X[:, :, :]).then_inc(o_store, 16)

            with act.Fori(0, DEPTH) as l:
                for k in range(KD):
                    if k >= 2:
                        alone(act, n_xr, l * KD + (k + 1), n_lo, l * KD + (k - 1))
                    else:
                        alone(act, n_xr, l * KD + (k + 1))
                    for lo_, hi_, which in SEGMENTS:
                        ins = act.activation(n_h[:, k % 2, lo_:hi_], n_t[:, k % 2, lo_:hi_], ACT.Identity,
                                             bias=mod[:, l, k, which:which + 1],
                                             scale=amul[:, l, k, which:which + 1])
                    ins.then_inc(n_aff, 1)
                    act.drain()
                    act.activation(h_hi[:, k, :], n_h[:, k % 2, :], ACT.Copy).then_inc(n_hi, 1)

                act.wait_ge(o_store, l * (32 * KD) + 16)
                def head(h, hh):
                    a = l * HEADS + h
                    n0 = l * NBLK + h * 5
                    act.dma_start(a_sf[:, 0, :], state_in[l, 0, h]).then_inc(a_s_in, 16)
                    act.dma_start(a_sb[:, CL - 1, :], state_in[l, 1, h]).then_inc(a_s_in, 16)
                    act.wait_ge(z_done, l * 12 + h)
                    for t in range(NT):
                        act.wait_ge(tile_done[t], n0 + 2)
                        act.activation(a_sig[:, t, :], ps[:, t, 0:TILE], ACT.Sigmoid).then_inc(a_act, 1)
                    for d, (f, kk) in enumerate(((a_ff, a_kf), (a_fb, a_kb))):
                        for t in range(NT):
                            cs = slice(t * TILE, (t + 1) * TILE)
                            act.wait_ge(tile_done[t], n0 + (d + 3))
                            act.activation(f[:, cs], ps[:, t, 0:TILE], ACT.Sigmoid)
                            act.activation(kk[:, cs], ps[:, t, 0:TILE], ACT.Sigmoid, scale=-1.0)\
                               .then_inc(tile_free[t], 1)
                        act.drain()
                        act.sem_inc(a_act, 1)

                    def mix(lev):
                        act.wait_ge(a_kup, a * 8 + lev + 1)
                        if lev >= 2:
                            act.wait_ge(a_mm, a * UNITS + (unit_at["level", lev - 2, 2] + 1))
                        v = lambda x: x.rearrange("p (b two j) -> p b two j", two=2, j=1 << lev)
                        for side, k in enumerate((a_kf, a_kb)):
                            ins = act.activation(v(a_km[:, lev % 2, :])[:, :, side, :],
                                                 v(k)[:, :, side, :], ACT.Copy)
                        ins.then_inc(a_mix, 1)

                    mix(0)
                    for t in range(NT):
                        act.wait_ge(tile_done[t], n0 + 5)
                        act.activation(a_vt[:, t * TILE:(t + 1) * TILE], ps[:, t, 0:TILE], ACT.Copy)\
                           .then_inc(tile_free[t], 1)
                    act.drain()
                    act.sem_inc(a_vt_s, 1)
                    for i, (kind, lev, g) in enumerate(units):
                        src = ps[:, 3 + i % 5, 0:TILE]
                        at3 = a_at[:, g * TILE:(g + 1) * TILE].rearrange("p (c t) -> p c t", c=3)
                        src3 = src.rearrange("p (c t) -> p c t", c=3)
                        if kind in ("vtok", "ktf", "ktb"):
                            act.wait_ge(a_mm, a * UNITS + (i + 1))
                            dst = {"vtok": a_v, "ktf": a_ktf, "ktb": a_ktb}[kind]
                            act.activation(dst[:, 3 * g:3 * g + 3, :], src3, ACT.Copy)\
                               .then_inc(a_vtok if kind == "vtok" else a_kt_s, 1)
                        if kind == "level" and g == 0 and lev + 1 < LEVELS:
                            mix(lev + 1)
                        if (kind, lev, g) == ("level", MASKS, 0):
                            act.wait_ge(a_asm, a + 1)
                        if kind == "level" and lev >= MASKS:
                            act.wait_ge(a_mm, a * UNITS + (i + 1))
                            half = 1 << lev
                            for b in range(P // half):
                                s0, t0 = b * half, (b ^ 1) * half
                                act.activation(at3[s0:s0 + half, :, t0:t0 + half],
                                               src3[s0:s0 + half, :, t0:t0 + half], ACT.Copy)
                        if kind in ("vtok", "ktf", "ktb") or (kind == "level" and lev >= MASKS):
                            act.drain()
                            act.sem_inc(a_free[i % 5], 1)
                        if (kind, lev, g) == ("level", LEVELS - 1, 2):
                            act.sem_inc(a_asm_act, 1)
                        if kind == "level" and lev in (2, 4, 6) and g == 2:
                            t = lev // 2 - 1
                            act.wait_ge(tile_done[t], n0 + 6)
                            act.activation(a_sig[:, t, :], ps[:, t, 0:TILE], ACT.Silu).then_inc(tile_free[t], 1)
                    act.wait_ge(a_fin_s, a + 1)
                    act.dma_start(state_out[l, h], a_fin[:, :, :]).then_inc(a_fin_out, 16)
                    for g in range(3):
                        i = unit_at["out", 0, g]
                        act.wait_ge(a_mm, a * UNITS + (i + 1))
                        act.activation(a_sq[:, g * TILE:(g + 1) * TILE], ps[:, 3 + i % 5, 0:TILE],
                                       ACT.Square).then_inc(z_sq_s, 1)
                        act.activation(X[:, h, g * TILE:(g + 1) * TILE], ps[:, 3 + i % 5, 0:TILE],
                                       ACT.Copy).then_inc(a_free[i % 5], 1)
                    act.drain()
                    act.sem_inc(z_act, 1)
                    act.preload_act_table_set("natural_log_exp_and_others")
                    for g in range(3):
                        i = unit_at["sum", 0, g]
                        act.wait_ge(a_mm, a * UNITS + (i + 1))
                        rstd(a_rs[:, g * TILE:(g + 1) * TILE], 3 + i % 5, 1.0 / P, z_rs_s)
                        act.sem_inc(a_free[i % 5], 1)

                with act.Fori(0, HEADS // 2) as hp:
                    for hh in range(2):
                        head(hp * 2 + hh, hh)

                def tails(n_first, count0, src0, normed):
                    def squares(s):
                        for t in range(NT):
                            cs = slice(t * TILE, (t + 1) * TILE)
                            act.activation(z_sq[:, s % 2, cs], X[:, src0 + s, cs], ACT.Square)\
                               .then_inc(z_sq_s, 1)

                    act.drain()
                    if normed:
                        squares(0)
                    for s in range(HEADS):
                        if normed:
                            act.preload_act_table_set("natural_log_exp_and_others")
                        if s >= 2:
                            act.wait_ge(z_done, l * 12 + (count0 // 3 + s - 1))
                        if normed:
                            for t in range(NT):
                                act.wait_ge(z_sum, l * 12 + (count0 - 12 + 3 * s + t + 1))
                                rstd(z_rs[:, s % 2, t * TILE:(t + 1) * TILE], 3 + t, 1.0 / P, z_rs_s)
                            if s + 1 < HEADS:
                                squares(s + 1)
                        for t in range(NT):
                            act.wait_ge(tile_done[t], l * NBLK + (n_first + s + 2))
                            act.activation(z_sz[:, s % 2, t * TILE:(t + 1) * TILE], ps[:, t, 0:TILE],
                                           ACT.Silu).then_inc(tile_free[t], 1)
                        act.drain()
                        act.sem_inc(z_act, 1)

                act.preload_act_table_set("natural_log_exp_and_others")
                act.wait_ge(z_done, l * 12 + 4)
                with act.Fori(0, HEADS // 2) as hp:
                    for hh in range(2):
                        h = hp * 2 + hh
                        a = l * HEADS + (hp * 2 + hh)
                        n0 = l * NBLK + (hp * 6 + (B0 + 3 * hh))
                        act.dma_start(b_rope[:, :, :], rope).then_inc(rope_in, 16)
                        act.dma_start(b_k[:, T_LAT:T], cache_k[l, h]).then_inc(b_cache, 16)
                        act.dma_start(b_v[:, CL, :], cache_v[l, h]).then_inc(b_cache, 16)
                        for m, (raw, sq) in enumerate(((b_raw, b_sq), (b_raw2, b_sq2))):
                            for t in range(NT):
                                cs = slice(t * TILE, (t + 1) * TILE)
                                act.wait_ge(tile_done[t], n0 + (m + 2))
                                act.activation(sq[:, cs], ps[:, t, 0:TILE], ACT.Square).then_inc(b_raw_s, 1)
                                act.activation(raw[:, cs], ps[:, t, 0:TILE], ACT.Copy).then_inc(tile_free[t], 1)
                        for m, (rs, banks) in enumerate(((b_rs, (3, 4, 5)), (b_rs2, (6, 7, 3)))):
                            for t in range(NT):
                                act.wait_ge(b_sum, a * 6 + (3 * m + t + 1))
                                rstd(rs[:, t * TILE:(t + 1) * TILE], banks[t], 1.0 / DH_B, b_rs_s)
                        own = [slice(m * DH_B, (m + 1) * DH_B) for m in range(2)]

                        def value_tile(t):
                            act.wait_ge(tile_done[t], n0 + 4)
                            act.activation(b_vt[:, t * TILE:(t + 1) * TILE], ps[:, t, 0:TILE], ACT.Copy)\
                               .then_inc(tile_free[t], 1)

                        value_tile(0)
                        act.wait_ge(b_qk, a * 2 + 1)
                        for m in range(2):
                            ins = act.activation(b_qs[own[m], m, :], b_q[own[m], :], ACT.Copy)
                        ins.then_inc(b_hi, 1)
                        value_tile(1)
                        act.wait_ge(b_cache, 32 * a + 32)
                        act.wait_ge(b_qk, a * 2 + 2)
                        for m in range(2):
                            ins = act.activation(b_kh[own[m], m, :], b_k[own[m], :], ACT.Copy)
                        ins.then_inc(b_hi, 1)
                        value_tile(2)
                        act.drain()
                        act.sem_inc(b_vt_s, 1)
                        for m in range(2):
                            ins = act.activation(b_kh[own[1 - m], m, :], b_k[own[m], :], ACT.Copy)
                        ins.then_inc(b_hi, 1)
                        act.wait_ge(b_qn, a * 2 + 2)
                        act.dma_start(k_out[l, h], b_n[:, 1, T_LAT:T]).then_inc(b_kv_out, 16)
                        act.dma_start(v_out[l, h], b_vt[:, T_LAT:T]).then_inc(b_kv_out, 16)
                        for g in range(3):
                            act.wait_ge(b_vtr, a * 3 + (g + 1))
                            src = ps[:, g, 0:TILE].rearrange("p (c t) -> p c t", c=3)
                            if g < 2:
                                act.activation(b_v[:, 3 * g:3 * g + 3, :], src, ACT.Copy).then_inc(b_vtok, 1)
                            else:
                                act.activation(b_v[:, 6:8, :], src[:, 0:2, :], ACT.Copy)
                                act.activation(b_v[:, CH, :], src[:, 2, :], ACT.Copy)
                                act.drain()
                                act.sem_inc(b_vtok, 1)
                        act.wait_ge(b_kv_out, 32 * a + 32)
                        ring = 0

                        def weights_read(i, g):
                            nonlocal ring
                            act.wait_ge(b_tr, a * 30 + (ring + 1))
                            half, k = (i % 2) * P, 1 if i == CTX else 3
                            act.activation(b_wt[:, 3 * g:3 * g + k, half:half + P],
                                           ps[:, 6 + ring % 2, 0:k * P].rearrange("p (c t) -> p c t", c=k),
                                           ACT.Copy).then_inc(b_ev, 1)
                            ring += 1

                        def values_read(i):
                            nonlocal ring
                            first, wide = (i * P, P) if i == CTX else ((i - 1) * P, 2 * P)
                            alone(act, b_tr, a * 30 + (ring + 1))
                            act.activation(X[:, hp * 2 + (4 + hh), first:first + wide],
                                           ps[:, 6 + ring % 2, 0:wide], ACT.Copy).then_inc(b_ev, 1)
                            ring += 1

                        def exponentials(i, m):
                            act.wait_ge(b_max, a * 18 + (2 * i + m + 1))
                            if i == CTX:
                                src, dst = ps[:, 3 * m, 0:P], b_p[i % 3][:, m, 0:P]
                            else:
                                src = ps[:, 3 * m:3 * m + 3, 0:TILE]
                                dst = b_p[i % 3][:, m, :].rearrange("p (a b) -> p a b", a=NT)
                            act.activation(dst, src, ACT.Exp, bias=stat[:, i % 3, m:m + 1],
                                           accum_out=stat[:, i % 3, 2 + m:3 + m]).then_inc(b_exp, 1)

                        for i in range(CH):
                            exponentials(i, 0)
                            if i % 2 == 0 and i >= 4:
                                values_read(i - 3)
                            if i >= 2:
                                for g in range(3):
                                    weights_read(i - 2, g)
                            exponentials(i, 1)
                        for g in range(3):
                            weights_read(CTX - 1, g)
                        values_read(CTX - 1)
                        weights_read(CTX, 0)
                        values_read(CTX)
                tails(ZB0, 12, 4, True)

                def split_y(src, order):
                    act.wait_ge(z_done, l * 12 + (8, 8, 12)[order])
                    for k in range(HEADS):
                        act.activation(y_hi[:, k, :], src[:, k, :], ACT.Copy).then_inc(y_hi_s, 1)

                def merge(n_first, order):
                    with act.Fori(0, KD) as j:
                        n = l * NBLK + (j * 2 + n_first)
                        for t in range(NT):
                            act.wait_ge(tile_done[t], n + 2)
                            act.wait_ge(m_done, l * 72 + (j * 3 + 24 * order))
                            act.activation(m_g[:, t, :], ps[:, t, 0:TILE], ACT.Sigmoid).then_inc(tile_free[t], 1)
                        act.drain()
                        act.sem_inc(m_gate, 1)

                split_y(X, 0)
                merge(MA0, 0)
                act.wait_ge(tile_done[NT - 1], l * NBLK + (MB0 + 1))
                split_y(yb, 1)
                merge(MB0, 1)

                act.wait_ge(tile_done[NT - 1], l * NBLK + (C0 + 1))
                act.wait_ge(m_done, l * 72 + 48)
                act.dma_start(c_t[:, :, :], dft_t).then_inc(c_tab, 16)
                act.dma_start(c_c[:, :, :, :], dft_c).then_inc(c_tab, 16)
                with act.Fori(0, HEADS // 2) as gp:
                    for s in range(2):
                        n = l * NBLK + (gp * 2 + (C0 + s))
                        for t in range(NT):
                            act.wait_ge(tile_done[t], n + 2)
                            act.activation(c_u[:, s, t * TILE:(t + 1) * TILE], ps[:, t, 0:TILE],
                                           ACT.Copy).then_inc(tile_free[t], 1)
                        act.drain()
                        act.sem_inc(c_u_s, 1)
                    for s in range(2):
                        g1 = l * HEADS + (gp * 2 + s)
                        for d2 in range(4):
                            act.wait_ge(c_mm, g1 * 5 + (d2 + 1))
                            act.activation(c_ri[:, 2 * d2:2 * d2 + 2, :], ps[:, 3 + d2, :]
                                           .rearrange("p (a b) -> p a b", a=2), ACT.Copy).then_inc(c_ri_s, 1)
                        act.wait_ge(c_mm, g1 * 5 + 5)
                        act.activation(c_ri[:, CTX, :], ps[:, 7, 0:256], ACT.Copy).then_inc(c_ri_s, 1)
                        for q in range(2):
                            dst = yb[:, gp * 2 + s, 0:T_LAT].rearrange("p (c d) -> p d c", d=8)[:, 4 * q:4 * q + 4, :]
                            alone(act, c_fin, g1 * 3 + (q + 1))
                            act.activation(dst, ps[:, 3 + q, :].rearrange("p (d c) -> p d c", d=4),
                                           ACT.Copy).then_inc(c_out, 1)
                        alone(act, c_fin, g1 * 3 + 3)
                        act.activation(yb[:, gp * 2 + s, T_LAT:T], ps[:, 5, 0:P], ACT.Copy).then_inc(c_out, 1)
                act.drain()
                tails(ZC0, 24, 0, False)
                split_y(yb, 2)
                merge(MC0, 2)

                act.wait_ge(tile_done[NT - 1], l * NBLK + (O0 + 1))
                act.wait_ge(o_store, l * (32 * KD) + 16)
                act.dma_start(x_res[:, :, :], x_keep.rearrange("k p t -> p k t")).then_inc(o_xin, 16)
                act.wait_ge(m_done, l * 72 + 72)
                for k in range(KD):
                    act.activation(h_hi[:, k, :], X[:, k, :], ACT.Copy).then_inc(o_hi, 1)
                for j in range(KD):
                    act.wait_ge(o_res, l * KD + (j + 1))
                    act.dma_start(x_keep[j], X[:, j, :]).then_inc(o_store, 16)
                    act.dma_start(x_out[:, j, :], X[:, j, :]).then_inc(o_store, 16)
                    norm_square(l * KD + KD, j, X[:, j, :])
                norm_rstd(l * KD + KD)
            act.wait_ge(o_store, 32 * KD * DEPTH + 16)
            act.wait_ge(a_fin_out, 16 * HEADS * DEPTH)
            act.wait_ge(b_kv_out, 32 * HEADS * DEPTH)

        @block.vector
        def _(dve):
            dve.memset(epsc[:, :], EPS).then_inc(eps_set, 1)
            dve.wait_ge(const_in, 48)
            dve.tensor_copy(mask[:, :, :], mask_in[:, :, :])
            lbp = par[:, PC_LB:PC_LB + 16].rearrange("p (l d h) -> p l d h", l=2, d=2)
            dve.tensor_tensor(lbt[:, 2, :, :], lbp[:, 0], lbp[:, 1], ALU.max)
            dve.drain()
            for l in range(DEPTH):
                ins = dve.tensor_tensor(lbt[:, l, :, :], lbp[:, l], lbt[:, 2, :, :], ALU.subtract)
            ins.then_inc(lb_sub, 1)
            lp = par[:, PC_LAM:PC_LAM + DEPTH * 4 * DH_B].rearrange("p (l a c) -> p l a c", l=DEPTH, a=4)
            for l in range(DEPTH):
                dve.tensor_tensor(lamw[:, l, :, :], lp[:, l, 0::2, :], lp[:, l, 1::2, :], ALU.mult)
            dve.drain()
            dve.tensor_reduce(lams[:, :, :], lamw[:, :, :, :], AX.X, ALU.add).then_inc(lam_dot, 1)
            dve.wait_ge(lb_exp, 1)
            dve.tensor_tensor(lbt[:, 2, :, :], lbt[:, 0, :, :], lbt[:, 1, :, :], ALU.add)
            dve.drain()
            dve.reciprocal(lbt[:, 3, :, :], lbt[:, 2, :, :])
            dve.drain()
            for l in range(DEPTH):
                dve.tensor_tensor(lbt[:, l, :, :], lbt[:, l, :, :], lbt[:, 3, :, :], ALU.mult)
            dve.drain()
            dve.tensor_tensor(lbt[:, 2, :, :], lbt[:, 0, :, :], lbt[:, 1, :, :], ALU.add)
            dve.tensor_tensor(lbv[:, 0, :, :], lbt[:, 0, :, :], lbt[:, 0, :, :], ALU.subtract)
            dve.drain()
            dve.tensor_tensor(lbv[:, 1, :, :], lbt[:, 2, :, :], lbt[:, 0, :, :], ALU.subtract)
            dve.drain()
            dve.tensor_scalar(oml[:, :, :, :], lbv[:, :, :, :], -1.0, 1.0, ALU.mult, ALU.add)
            dve.tensor_scalar(gq[:, :], par[:, PC_QN:PC_QN + DEPTH], DH_B ** -0.5, None, ALU.mult)
            dve.tensor_scalar(gsub[:, :], par[:, PC_LI:PC_LI + DEPTH], -1.0, 1.0, ALU.mult, ALU.add)
            dve.drain()
            dve.tensor_tensor(gsub[:, :], gsub[:, :], par[:, PC_SG:PC_SG + DEPTH], ALU.mult)
            dve.wait_ge(lam_exp, 1)
            dve.tensor_tensor(lam_n[:, :], lams[:, :, 1], lams[:, :, 0], ALU.subtract)
            dve.drain()
            dve.tensor_tensor(lam_n[:, :], lam_n[:, :], par[:, PC_LI:PC_LI + DEPTH], ALU.subtract)
            for l in range(DEPTH):
                dve.wait_ge(ada_t, l + 1)
                ab = par[:, PC_AB + l * 24:PC_AB + (l + 1) * 24].unsqueeze(2).broadcast_to((P, 24, 2))
                dve.tensor_tensor(mod[:, l, :, :], ps[:, 6, 0:48].rearrange("p (j c) -> p j c", c=2), ab,
                                  ALU.add).then_inc(setup_done, 1)
                dve.drain()
                ng = par[:, PC_NG + l * KD:PC_NG + (l + 1) * KD].unsqueeze(2).broadcast_to((P, KD, 2))
                dve.tensor_scalar(amul[:, l, :, :], mod[:, l, KD:2 * KD, :], 1.0, None, ALU.add)
                dve.drain()
                dve.tensor_tensor(amul[:, l, :, :], amul[:, l, :, :], ng, ALU.mult)
            dve.drain()

            with dve.Fori(0, DEPTH) as l:
                dve.wait_ge(n_rs_s, l * NT + NT)

                def over_rms(k):
                    if k >= 2:
                        dve.wait_ge(n_aff, l * KD + (k - 1))
                    dve.tensor_tensor(n_t[:, k % 2, :], X[:, k, :], n_rs[:, :], ALU.mult).then_inc(n_xr, 1)

                over_rms(0)
                over_rms(1)
                for k in range(KD):
                    dve.wait_ge(n_hi, l * KD + (k + 1))
                    dve.tensor_tensor(h_lo[:, k, :], n_h[:, k % 2, :], h_hi[:, k, :].bitcast(F32),
                                      ALU.subtract).then_inc(n_lo, 1)
                    if k + 2 < KD:
                        over_rms(k + 2)

                def head(h, hh):
                    a = l * HEADS + h
                    for t in range(NT):
                        dve.wait_ge(a_act, a * 5 + (t + 1))
                        dve.tensor_tensor(a_q[:, t * TILE:(t + 1) * TILE], ps[:, t, 0:TILE],
                                          a_sig[:, t, :], ALU.mult).then_inc(tile_free[t], 1)
                    for d, (f, kk) in enumerate(((a_ff, a_kf), (a_fb, a_kb))):
                        dve.wait_ge(a_act, a * 5 + (d + 4))
                        ins = dve.tensor_scalar(kk[:, :], kk[:, :], oml[:, l, d, bass.ds(h, 1)], None, ALU.mult)
                        if d:
                            ins.then_inc(a_kup, 1)
                        dve.tensor_scalar(f[:, :], f[:, :], oml[:, l, d, bass.ds(h, 1)], lbv[:, l, d, bass.ds(h, 1)],
                                          ALU.mult, ALU.add)
                    dve.drain()
                    dve.tensor_tensor(a_kd[:, :], a_kf[:, :], a_kb[:, :], ALU.add)
                    dve.tensor_tensor(a_qf[:, :], a_q[:, :], a_ff[:, :], ALU.mult)
                    dve.tensor_tensor(a_qb[:, :], a_q[:, :], a_fb[:, :], ALU.mult).then_inc(a_qup, 1)

                    def sides(x, lev):
                        v = x[:, :].rearrange("p (b two j) -> p b two j", two=2, j=1 << lev)
                        return v[:, :, 0, :], v[:, :, 1, :]

                    def k_up(lev):
                        dve.wait_ge(a_mix, a * LEVELS + (lev + 1))
                        shape = (P, T >> (lev + 1), 1 << lev)
                        (f_l, f_r), (b_l, b_r) = sides(a_ff, lev), sides(a_fb, lev)
                        k_l, k_r = sides(a_kf, lev)[0], sides(a_kb, lev)[1]
                        dve.tensor_tensor(k_l, k_l, f_r[:, :, 0:1].broadcast_to(shape), ALU.mult)
                        dve.tensor_tensor(k_r, k_r, b_l[:, :, 0:1].broadcast_to(shape), ALU.mult)\
                           .then_inc(a_kup, 1)

                    def q_up(lev):
                        dve.wait_ge(a_mm, a * UNITS + (unit_at["level", lev, 2] + 1))
                        shape = (P, T >> (lev + 1), 1 << lev)
                        (f_l, f_r), (b_l, b_r) = sides(a_ff, lev), sides(a_fb, lev)
                        q_r, q_l = sides(a_qf, lev)[1], sides(a_qb, lev)[0]
                        dve.tensor_tensor(q_r, q_r, f_l[:, :, 0:1].broadcast_to(shape), ALU.mult)
                        dve.tensor_tensor(q_l, q_l, b_r[:, :, 0:1].broadcast_to(shape), ALU.mult)\
                           .then_inc(a_qup, 1)
                        dve.drain()
                        dve.tensor_tensor(f_l[:, :, 0:1], f_l[:, :, 0:1], f_r[:, :, 0:1], ALU.mult)
                        dve.tensor_tensor(b_l[:, :, 0:1], b_l[:, :, 0:1], b_r[:, :, 0:1], ALU.mult)
                        dve.drain()

                    def masked(kind, lev, g, table):
                        i = unit_at[kind, lev, g]
                        alone(dve, a_mm, a * UNITS + (i + 1))
                        dve.copy_predicated(
                            a_at[:, g * TILE:(g + 1) * TILE].rearrange("p (c t) -> p c t", c=3),
                            mask[:, table, :].unsqueeze(1).broadcast_to((P, 3, P)),
                            ps[:, 3 + i % 5, 0:TILE].rearrange("p (c t) -> p c t", c=3))\
                           .then_inc(a_free[i % 5], 1)

                    dve.drain()
                    k_up(0)
                    for g in range(3):
                        masked("diag", 0, g, MASKS)
                    for lev in range(LEVELS):
                        if lev:
                            k_up(lev)
                        q_up(lev)
                        if lev < MASKS:
                            for g in range(3):
                                masked("level", lev, g, lev)
                        if lev == MASKS - 1:
                            dve.drain()
                            dve.sem_inc(a_asm, 1)
                    for d, f in enumerate((a_ff, a_fb)):
                        dve.tensor_copy(ptot[:, d, :], f[:, 0:T:P])
                    dve.drain()
                    dve.wait_ge(a_s_in, 32 * a + 32)
                    dve.wait_ge(a_fin_out, 16 * a)
                    for g in range(3):
                        i = unit_at["uf", 0, g]
                        dve.wait_ge(a_mm, a * UNITS + (i + 1))
                        for c in range(3 * g, 3 * g + 3):
                            u = ps[:, 3 + i % 5, (c % 3) * P:(c % 3 + 1) * P]
                            if c < CL - 1:
                                dve.scalar_tensor_tensor(a_sf[:, c + 1, :], a_sf[:, c, :], ptot[:, 0, c:c + 1],
                                                         u, ALU.mult, ALU.add)
                                dve.drain()
                            elif c == CTX:
                                dve.tensor_copy(a_fin[:, 0, :], u)
                        dve.drain()
                        dve.sem_inc(a_free[i % 5], 1)
                    for g in range(3):
                        i = unit_at["ub", 0, g]
                    banks = [3 + unit_at["ub", 0, g] % 5 for g in range(3)]
                    dve.wait_ge(a_mm, a * UNITS + (unit_at["ub", 0, 2] + 1))
                    dve.tensor_copy(a_fin[:, 1, :], ps[:, banks[2], 2 * P:3 * P])
                    for c in range(CL - 1, 0, -1):
                        dve.scalar_tensor_tensor(a_sb[:, c - 1, :], a_sb[:, c, :], ptot[:, 1, c:c + 1],
                                                 ps[:, banks[c // 3], (c % 3) * P:(c % 3 + 1) * P],
                                                 ALU.mult, ALU.add)
                        dve.drain()
                    for g in range(3):
                        dve.sem_inc(a_free[banks[g] - 3], 1)
                    dve.sem_inc(a_st, 1)
                    dve.sem_inc(a_fin_s, 1)
                    dve.wait_ge(z_act, l * 12 + (h + 1))
                    dve.wait_ge(z_rs_s, l * 24 + (h * 3 + 3))
                    g = par[:, bass.ds(l * HEADS + (h + PC_HG), 1)]
                    dve.scalar_tensor_tensor(X[:, h, :], X[:, h, :], g, a_rs[:, :], ALU.mult, ALU.mult)
                    dve.drain()
                    dve.tensor_tensor(X[:, h, :], X[:, h, :], a_sig[:, :, :].rearrange("p a b -> p (a b)"),
                                      ALU.mult).then_inc(z_done, 1)

                with dve.Fori(0, HEADS // 2) as hp:
                    for hh in range(2):
                        head(hp * 2 + hh, hh)

                def tails(src, src0, dst, count0, normed):
                    for s in range(HEADS):
                        o, y = src[:, src0 + s, :], dst[:, s, :]
                        if normed:
                            dve.wait_ge(z_rs_s, l * 24 + (count0 * 3 + 3 * s + 3))
                            dve.scalar_tensor_tensor(y, o, gsub[:, bass.ds(l, 1)], z_rs[:, s % 2, :], ALU.mult, ALU.mult)
                            dve.drain()
                            o = y
                        dve.wait_ge(z_act, l * 12 + (count0 + s + 1))
                        dve.tensor_tensor(y, o, z_sz[:, s % 2, :], ALU.mult).then_inc(z_done, 1)

                with dve.Fori(0, HEADS // 2) as hp:
                    for hh in range(2):
                        a = l * HEADS + (hp * 2 + hh)
                        for m, (raw, rs, dst) in enumerate(((b_raw, b_rs, b_q), (b_raw2, b_rs2, b_k))):
                            gain = gq[:, bass.ds(l, 1)] if m == 0 else par[:, bass.ds(l + PC_KN, 1)]
                            dve.wait_ge(b_rs_s, a * 6 + (3 * m + 3))
                            dve.scalar_tensor_tensor(b_n[:, m, :], raw[:, :], gain, rs[:, :],
                                                     ALU.mult, ALU.mult).then_inc(b_qn, 1)
                            dve.drain()
                            if m == 0:
                                dve.wait_ge(rope_in, a * 16 + 16)
                            dve.tensor_tensor(dst[:, 0:T_LAT], b_n[:, m, 0:T_LAT], b_rope[:, 0, :], ALU.mult)
                            ctx_at = T_LAT if m == 0 else T
                            dve.tensor_copy(dst[:, ctx_at:ctx_at + P], b_n[:, m, T_LAT:T])
                        for m, dst in enumerate((b_q, b_k)):
                            dve.wait_ge(b_rot, a * 4 + (2 * m + 2))
                            dve.tensor_tensor(b_rc[:, :].rearrange("p (a b) -> p a b", a=2),
                                              ps[:, 4 + 2 * m:6 + 2 * m, :],
                                              b_rope[:, 1, :].rearrange("p (a b) -> p a b", a=2), ALU.mult)
                            dve.drain()
                            dve.tensor_tensor(dst[:, 0:T_LAT], dst[:, 0:T_LAT], b_rc[:, :], ALU.add)\
                               .then_inc(b_qk, 1)
                            dve.drain()
                        halves = [slice(x * DH_B, (x + 1) * DH_B) for x in range(2)]
                        dve.wait_ge(b_hi, a * 3 + 1)
                        for m in range(2):
                            dve.tensor_tensor(b_qs[halves[1 - m], m, :], b_q[halves[m], :],
                                              b_qs[halves[m], m, :].bitcast(F32), ALU.subtract)
                        dve.wait_ge(b_hi, a * 3 + 2)
                        for m in range(2):
                            ins = dve.tensor_tensor(b_kl[halves[m], :], b_k[halves[m], :],
                                                    b_kh[halves[m], m, :].bitcast(F32), ALU.subtract)
                        ins.then_inc(b_lo, 1)

                        def greatest(i, m):
                            dve.wait_ge(b_sc, a * 18 + (2 * i + m + 1))
                            src = ps[:, 3 * m, 0:P] if i == CTX else ps[:, 3 * m:3 * m + 3, 0:TILE]
                            dve.tensor_reduce(stat[:, i % 3, m:m + 1], src, AX.X if i == CTX else AX.XY,
                                              ALU.max, negate=True).then_inc(b_max, 1)

                        def weights(i):
                            e, p, wide = i % 3, b_p[i % 3], P if i == CTX else T
                            dve.wait_ge(b_exp, a * 18 + (2 * i + 2))
                            dve.reciprocal(stat[:, e, 4:6], stat[:, e, 2:4])
                            dve.drain()
                            dve.tensor_tensor(stat[:, e, 6:7], stat[:, e, 5:6], lam_n[:, bass.ds(l, 1)], ALU.mult)
                            dve.tensor_scalar(p[:, 0, 0:wide], p[:, 0, 0:wide], stat[:, e, 4:5], None, ALU.mult)
                            dve.drain()
                            dve.scalar_tensor_tensor(p[:, 0, 0:wide], p[:, 1, 0:wide], stat[:, e, 6:7],
                                                     p[:, 0, 0:wide], ALU.mult, ALU.add).then_inc(b_w, 1)

                        for i in range(CH):
                            greatest(i, 0)
                            if i:
                                weights(i - 1)
                            greatest(i, 1)
                        weights(CTX)
                tails(X, 4, yb, 4, True)

                def split_y(src, order):
                    for k in range(HEADS):
                        dve.wait_ge(y_hi_s, l * 12 + (4 * order + k + 1))
                        dve.tensor_tensor(y_lo[:, k, :], src[:, k, :], y_hi[:, k, :].bitcast(F32),
                                          ALU.subtract).then_inc(y_lo_s, 1)

                def merge(n_first, order):
                    with dve.Fori(0, KD) as j:
                        n = l * NBLK + (j * 2 + n_first)
                        dve.wait_ge(m_gate, l * 24 + (j + (8 * order + 1)))
                        for t in range(NT):
                            cs = slice(t * TILE, (t + 1) * TILE)
                            dve.wait_ge(tile_done[t], n + 3)
                            if order == 0:
                                dve.tensor_tensor(X[:, j, cs], ps[:, t, 0:TILE], m_g[:, t, :],
                                                  ALU.mult).then_inc(tile_free[t], 1)
                            else:
                                dve.tensor_tensor(m_p[:, t, :], ps[:, t, 0:TILE], m_g[:, t, :],
                                                  ALU.mult).then_inc(tile_free[t], 1)
                        dve.drain()
                        for t in range(NT):
                            cs = slice(t * TILE, (t + 1) * TILE)
                            if order:
                                dve.tensor_tensor(X[:, j, cs], X[:, j, cs], m_p[:, t, :], ALU.add)
                        dve.drain()
                        for t in range(NT):
                            dve.sem_inc(m_done, 1)

                split_y(X, 0)
                merge(MA0, 0)
                split_y(yb, 1)
                merge(MB0, 1)

                R = math.sqrt(0.5)
                with dve.Fori(0, HEADS // 2) as gp:
                    for s in range(2):
                        g1 = l * HEADS + (gp * 2 + s)
                        u = c_u[:, s, 0:T_LAT].rearrange("p (a b) -> p a b", a=8)
                        dve.wait_ge(c_u_s, g1 + 1)
                        dve.wait_ge(c_mm, g1 * 5)
                        dve.tensor_tensor(c_e[:, 0, :, :], u[:, 0:4], u[:, 4:8], ALU.add)
                        dve.tensor_tensor(c_e[:, 1, :, :], u[:, 0:4], u[:, 4:8], ALU.subtract)
                        dve.drain()
                        even, odd = c_e[:, 0], c_e[:, 1]
                        dve.tensor_tensor(c_s[:, 0:2, :], even[:, 0:2], even[:, 2:4], ALU.add)
                        dve.tensor_tensor(c_z[:, 6:8, :], even[:, 0:2], even[:, 2:4], ALU.subtract)
                        dve.tensor_tensor(c_s[:, 2, :], odd[:, 1], odd[:, 3], ALU.subtract)
                        dve.tensor_tensor(c_s[:, 3, :], odd[:, 1], odd[:, 3], ALU.add)
                        dve.drain()
                        dve.tensor_tensor(c_z[:, 0, :], c_s[:, 0], c_s[:, 1], ALU.add)
                        dve.tensor_tensor(c_z[:, 1, :], c_s[:, 0], c_s[:, 1], ALU.subtract)
                        dve.scalar_tensor_tensor(c_z[:, 2, :], c_s[:, 2], R, odd[:, 0], ALU.mult, ALU.add)
                        dve.scalar_tensor_tensor(c_z[:, 3, :], c_s[:, 2], -R, odd[:, 0], ALU.mult, ALU.add)
                        dve.scalar_tensor_tensor(c_z[:, 4, :], c_s[:, 3], R, odd[:, 2], ALU.mult, ALU.add)
                        dve.scalar_tensor_tensor(c_z[:, 5, :], c_s[:, 3], -R, odd[:, 2], ALU.mult, ALU.add)
                        dve.drain()
                        dve.sem_inc(c_z_s, 1)
                alone(dve, c_out, l * 12 + 12)
                tails(yb, 0, yb, 8, False)
                split_y(yb, 2)
                merge(MC0, 2)

                for k in range(KD):
                    dve.wait_ge(o_hi, l * KD + (k + 1))
                    dve.tensor_tensor(h_lo[:, k, :], X[:, k, :], h_hi[:, k, :].bitcast(F32),
                                      ALU.subtract).then_inc(o_lo, 1)
                alone(dve, o_xin, l * 16 + 16)
                with dve.Fori(0, KD) as j:
                    n = l * NBLK + (j + O0)
                    for t in range(NT):
                        dve.wait_ge(tile_done[t], n + 2)
                        for lo_, hi_, which in SEGMENTS:
                            lo_, hi_ = max(lo_, t * TILE), min(hi_, (t + 1) * TILE)
                            if lo_ >= hi_:
                                continue
                            ins = dve.scalar_tensor_tensor(
                                X[:, j, lo_:hi_], ps[:, t, lo_ - t * TILE:hi_ - t * TILE],
                                mod[:, l, j + 2 * KD, which:which + 1], x_res[:, j, lo_:hi_], ALU.mult, ALU.add)
                        ins.then_inc(tile_free[t], 1)
                    dve.drain()
                    dve.sem_inc(o_res, 1)
                dve.drain()


def square_constants():
    ident = np.eye(P, dtype=np.float32)
    ones = np.ones((P, P), np.float32)
    head_ones = np.kron(np.eye(2), np.ones((DH_B, DH_B))).astype(np.float32)
    rot = np.zeros((P, P), np.float32)
    nf = DH_B // 4
    for b in range(0, P, 2 * nf):
        for i in range(nf):
            rot[b + nf + i, b + i] = -1.0
            rot[b + i, b + nf + i] = 1.0
    return np.ascontiguousarray(np.stack([ident, ones, head_ones, rot], axis=1))


def level_masks():
    s, t = np.meshgrid(np.arange(P), np.arange(P), indexing="ij")
    out = []
    for lev in range(MASKS):
        half = 1 << lev
        same = (s // (2 * half)) == (t // (2 * half))
        out.append(same & (s // half != t // half))
    out.append(s == t)
    return np.ascontiguousarray(np.stack(out, axis=1).astype(np.float32))


def rope_tables():
    nf = DH_B // 4
    inv = (np.float32(ROPE_BASE) ** (-np.arange(nf, dtype=np.float32) / np.float32(nf))).astype(np.float32)
    tok = np.arange(T_LAT)
    row, colm = (tok // GRID_W).astype(np.float32), (tok % GRID_W).astype(np.float32)
    ang = np.concatenate([row[None, :] * inv[:, None]] * 2 + [colm[None, :] * inv[:, None]] * 2, axis=0)
    ang = np.concatenate([ang, ang], axis=0)
    return np.ascontiguousarray(np.stack([np.cos(ang), np.sin(ang)], axis=1).astype(np.float32))


def dft_tables():
    k = np.arange(P)
    ang = 2 * np.pi * np.outer(k, k) / P
    c, s = np.cos(ang), np.sin(ang)
    t = np.stack([np.concatenate([c, -s], 1), np.concatenate([s, c], 1), np.concatenate([-s, -c], 1)], axis=1)
    cc = np.zeros((P, 2, CH, P))
    for d in range(8):
        th = 2 * np.pi * np.outer(k, 8 * k + d) / T_LAT
        cc[:, 0, d], cc[:, 1, d] = np.cos(th), np.sin(th)
    cc[:, :, 0:8] /= math.sqrt(T_LAT * P)
    cc[:, 0, CTX], cc[:, 1, CTX] = c / P, s / P
    return np.ascontiguousarray(t.astype(np.float32)), np.ascontiguousarray(cc.astype(np.float32))


def blocks_of(w, n_k):
    L, _, n = w.shape
    w = w.reshape(L, n_k, P, n // P, P)
    return w.transpose(0, 3, 2, 1, 4).reshape(L, n // P, P, n_k * P)


def kernel(x_prompt, x_sample, c, cache_diff_k, cache_diff_v, state_hgrn, c_ctx, ada_w, ada_b, norm_g,
           w_in, hgrn_lb, hgrn_norm_g, diff_qn_g, diff_kn_g, diff_lambda, diff_subln_g, w_branch_a,
           w_branch_b, w_branch_c, w_out):
    import concourse.bacc as bacc
    from concourse.bass_utils import run_bass_kernel_spmd

    L = DEPTH
    win = blocks_of(w_in, KD)
    sec = lambda i, n=4: win[:, i * 4:i * 4 + n]
    gate = lambda b: win[:, 44 + b * KD:44 + (b + 1) * KD]

    def heads(*which):
        return np.stack([sec(i) for i in which], axis=2).reshape(L, 4 * len(which), P, KD * P)

    w_full = np.concatenate([heads(0, 1, 2, 3, 4), heads(5, 6, 7), sec(8), gate(0), gate(1),
                             sec(9), sec(10), gate(2), blocks_of(w_out, KD)], axis=1)
    w_half = np.concatenate([blocks_of(w, 4) for w in (w_branch_a, w_branch_b, w_branch_c)], axis=1)

    cols = lambda v, n: v.reshape(-1, n, P).transpose(2, 0, 1).reshape(P, -1)
    two = lambda v: np.concatenate([v, v], axis=1).T
    lam_init = np.array([0.8 - 0.6 * math.exp(-0.3 * l) for l in range(L)], np.float32)
    params = np.concatenate([
        cols(hgrn_lb.reshape(L * 2, HEADS * P), HEADS), cols(norm_g, KD), cols(hgrn_norm_g, HEADS),
        two(diff_qn_g), two(diff_kn_g), diff_subln_g.T, cols(ada_b, 3 * KD),
        np.broadcast_to(diff_lambda.reshape(1, -1), (P, L * 4 * DH_B)),
        np.stack([c[0].reshape(KD, P).T, c_ctx.reshape(KD, P).T], axis=2).reshape(P, KD * 2),
        np.broadcast_to(lam_init[None, :], (P, L))], axis=1)
    assert params.shape == (P, PC_ALL)

    x_t = np.concatenate([x_sample[0].T, x_prompt[0].T], axis=1)
    dft_t, dft_c = dft_tables()
    ins = {
        "x_t": x_t.reshape(KD, P, T).transpose(1, 0, 2),
        "w_full": w_full, "w_half": w_half, "ada_w": ada_w, "params": params,
        "squares": square_constants(), "masks": level_masks(), "rope": rope_tables(),
        "dft_t": dft_t, "dft_c": dft_c,
        "cache_k": cache_diff_k[0].transpose(0, 2, 3, 4, 1).reshape(L, HEADS, P, T_CTX),
        "cache_v": cache_diff_v[0].transpose(0, 2, 1, 3),
        "state_in": state_hgrn[0],
    }
    outs = {"x_new": (P, KD, T), "k_new": (L, HEADS, P, T_CTX), "v_new": (L, HEADS, P, T_CTX),
            "state_new": (L, HEADS, P, 2, P)}
    nc = bacc.Bacc("TRN2", target_bir_lowering=False, num_devices=1)
    arrays, args = {}, []
    for name, v in ins.items():
        v = np.ascontiguousarray(v)
        arrays["in_" + name] = v
        args.append(nc.dram_tensor("in_" + name, v.shape, mybir.dt.from_np(v.dtype), kind="ExternalInput").ap())
    for name, shape in outs.items():
        args.append(nc.dram_tensor("out_" + name, shape, F32, kind="ExternalOutput").ap())
    mixer_kernel(nc, *args)
    got = run_bass_kernel_spmd(nc, [arrays], core_ids=[0]).results[0]
    x_new = got["out_x_new"].transpose(1, 0, 2).reshape(D_MODEL, T)
    k_new = got["out_k_new"].reshape(L, HEADS, 2, DH_B, T_CTX).transpose(0, 4, 1, 2, 3)
    v_new = got["out_v_new"].transpose(0, 3, 1, 2)
    s_new = got["out_state_new"].transpose(0, 3, 1, 2, 4)
    return (np.ascontiguousarray(x_new[:, T_LAT:].T)[None], np.ascontiguousarray(x_new[:, :T_LAT].T)[None],
            np.ascontiguousarray(k_new)[None], np.ascontiguousarray(v_new)[None],
            np.ascontiguousarray(s_new)[None])
```
